# Optimizing a Trainium2 kernel written in Bass

```python
import jax, jax.numpy as jnp
from jax import lax
import numpy as np

D_MODEL = 1024
BATCH = 1
SEQ = 1024
DEPTH = 1
DEC_BATCH = 1
DEC_SEQ = 32
PAST_LEN = 1024

CHUNK = 64
N_META = 16
HEAD_DIM = 64
FOX_HEADS = 8
SB_HEADS = 8
FOX_WIDTH = FOX_HEADS * HEAD_DIM
SB_WIDTH = SB_HEADS * HEAD_DIM
Q_BLOCK = 128
NORM_EPS = 1e-6
MASK_VALUE = -1e30

PEER_HEADS = 8
PEER_N_KEYS = 128
PEER_N_EXPERTS = PEER_N_KEYS * PEER_N_KEYS
PEER_DK = 256
PEER_HALF = PEER_DK // 2
PEER_TOPK = 16
PEER_BLOCK = 256

IN_SIZES = (FOX_WIDTH, FOX_WIDTH, FOX_WIDTH, FOX_HEADS, SB_WIDTH, SB_WIDTH, SB_WIDTH, D_MODEL, D_MODEL)
IN_WIDTH = sum(IN_SIZES)
SPLIT_POINTS = tuple(int(s) for s in np.cumsum(IN_SIZES)[:-1])

kernel_name = "gated_fox_stickbreak_peer_stream_step"

def rms_norm(x, g):
    xf = x.astype(jnp.float32)
    y = xf * lax.rsqrt(jnp.mean(xf * xf, axis=-1, keepdims=True) + NORM_EPS)
    return (y * g.astype(jnp.float32)).astype(x.dtype)

def sweep_query_blocks(block_fn, q_arrays, q_pos):
    lq = q_pos.shape[0]
    blk = min(Q_BLOCK, lq)
    nb = -(-lq // blk)
    pad = nb * blk - lq

    def to_blocks(a):
        a = jnp.pad(a, [(0, 0), (0, pad)] + [(0, 0)] * (a.ndim - 2))
        a = a.reshape(a.shape[0], nb, blk, *a.shape[2:])
        return jnp.moveaxis(a, 1, 0)

    blocks = tuple(to_blocks(a) for a in q_arrays)
    pos = jnp.pad(q_pos, (0, pad), constant_values=-1).reshape(nb, blk)
    out = lax.map(lambda args: block_fn(args[0], *args[1]), (pos, blocks))
    out = jnp.moveaxis(out, 0, 1)
    return out.reshape(out.shape[0], nb * blk, *out.shape[3:])[:, :lq]

def fox_attention(q, c_q, k, v, c_k, q_pos, k_pos):
    scale = HEAD_DIM ** -0.5
    ck_t = jnp.transpose(c_k, (0, 2, 1))

    def block(qpos, qb, cqb):
        s = jnp.einsum('bqhd,bkhd->bhqk', qb, k).astype(jnp.float32) * scale
        s = s + (jnp.transpose(cqb, (0, 2, 1))[..., None] - ck_t[:, :, None, :])
        valid = k_pos[None, :] <= qpos[:, None]
        p = jax.nn.softmax(jnp.where(valid, s, MASK_VALUE), axis=-1)
        return jnp.einsum('bhqk,bkhd->bqhd', p.astype(v.dtype), v)

    return sweep_query_blocks(block, (q, c_q), q_pos)

def stick_breaking_attention(q, k, v, q_pos, k_pos):
    scale = HEAD_DIM ** -0.5

    def block(qpos, qb):
        z = jnp.einsum('bqhd,bkhd->bhqk', qb, k).astype(jnp.float32) * scale
        valid = k_pos[None, :] < qpos[:, None]
        m = jnp.where(valid, jax.nn.log_sigmoid(-z), 0.0)
        tail = lax.cumsum(m, axis=3, reverse=True) - m
        a = jnp.where(valid, jnp.exp(jax.nn.log_sigmoid(z) + tail), 0.0)
        return jnp.einsum('bhqk,bkhd->bqhd', a.astype(v.dtype), v)

    return sweep_query_blocks(block, (q,), q_pos)

def token_mixers(n, fox_k_past, fox_v_past, fox_logf_past, sb_k_past, sb_v_past,
                 w_in, b_forget, fox_q_norm, fox_k_norm, w_o_fox, w_o_sb, w_out):
    bsz, lq, _ = n.shape
    past = fox_k_past.shape[1]
    proj = n @ w_in
    fq, fk, fv, ff, sq, sk, sv, ga, gb = jnp.split(proj, SPLIT_POINTS, axis=-1)
    heads = lambda t, h: t.reshape(bsz, lq, h, HEAD_DIM)
    fq = rms_norm(heads(fq, FOX_HEADS), fox_q_norm)
    fk = rms_norm(heads(fk, FOX_HEADS), fox_k_norm)
    fv = heads(fv, FOX_HEADS)
    logf = jax.nn.log_sigmoid((ff + b_forget).astype(jnp.float32))
    sq, sk, sv = heads(sq, SB_HEADS), heads(sk, SB_HEADS), heads(sv, SB_HEADS)

    q_pos = past + jnp.arange(lq, dtype=jnp.int32)
    k_pos = jnp.arange(past + lq, dtype=jnp.int32)
    fk_all = jnp.concatenate([fox_k_past.astype(fk.dtype), fk], axis=1)
    fv_all = jnp.concatenate([fox_v_past.astype(fv.dtype), fv], axis=1)
    c = jnp.cumsum(jnp.concatenate([fox_logf_past.astype(jnp.float32), logf], axis=1), axis=1)
    sk_all = jnp.concatenate([sb_k_past.astype(sk.dtype), sk], axis=1)
    sv_all = jnp.concatenate([sb_v_past.astype(sv.dtype), sv], axis=1)

    o_fox = fox_attention(fq, c[:, past:], fk_all, fv_all, c, q_pos, k_pos)
    o_sb = stick_breaking_attention(sq, sk_all, sv_all, q_pos, k_pos)
    y_fox = o_fox.reshape(bsz, lq, FOX_WIDTH) @ w_o_fox
    y_sb = o_sb.reshape(bsz, lq, SB_WIDTH) @ w_o_sb
    merged = jax.nn.sigmoid(ga) * y_fox + jax.nn.sigmoid(gb) * y_sb
    return merged @ w_out, (fk, fv, logf, sk, sv)

def peer_ffn(n, w_peer_q, sub_keys_1, sub_keys_2, expert_u, expert_v):
    shape = n.shape
    x = n.reshape(-1, D_MODEL)
    t = x.shape[0]
    blk = min(PEER_BLOCK, t)
    nb = -(-t // blk)
    xb = jnp.pad(x, ((0, nb * blk - t), (0, 0))).reshape(nb, blk, D_MODEL)

    def block(xt):
        q = (xt @ w_peer_q).reshape(blk, PEER_HEADS, 2, PEER_HALF)
        s1 = jnp.einsum('thc,nc->thn', q[:, :, 0], sub_keys_1).astype(jnp.float32)
        s2 = jnp.einsum('thc,nc->thn', q[:, :, 1], sub_keys_2).astype(jnp.float32)
        v1, i1 = lax.top_k(s1, PEER_TOPK)
        v2, i2 = lax.top_k(s2, PEER_TOPK)
        cand = (v1[..., :, None] + v2[..., None, :]).reshape(blk, PEER_HEADS, PEER_TOPK * PEER_TOPK)
        sc, ci = lax.top_k(cand, PEER_TOPK)
        e1 = jnp.take_along_axis(i1, ci // PEER_TOPK, axis=-1)
        e2 = jnp.take_along_axis(i2, ci % PEER_TOPK, axis=-1)
        eidx = e1 * PEER_N_KEYS + e2
        g = jax.nn.softmax(sc, axis=-1)
        act = jax.nn.gelu(jnp.einsum('thkd,td->thk', expert_u[eidx], xt), approximate=False)
        w = (g * act.astype(jnp.float32)).astype(expert_v.dtype)
        return jnp.einsum('thk,thkd->td', w, expert_v[eidx])

    out = lax.map(block, xb).reshape(nb * blk, D_MODEL)[:t]
    return out.reshape(shape).astype(n.dtype)

def layer_forward(x, fox_k_past, fox_v_past, fox_logf_past, sb_k_past, sb_v_past,
                  norm_mix, w_in, b_forget, fox_q_norm, fox_k_norm, w_o_fox, w_o_sb, w_out,
                  norm_ffn, w_peer_q, sub_keys_1, sub_keys_2, expert_u, expert_v):
    y, rows = token_mixers(rms_norm(x, norm_mix), fox_k_past, fox_v_past, fox_logf_past,
                           sb_k_past, sb_v_past, w_in, b_forget, fox_q_norm, fox_k_norm,
                           w_o_fox, w_o_sb, w_out)
    h = x + y
    out = h + peer_ffn(rms_norm(h, norm_ffn), w_peer_q, sub_keys_1, sub_keys_2, expert_u, expert_v)
    return out, rows

def run_stack(x, past_of_layer, weights):
    rows = []
    for layer in range(DEPTH):
        x, r = layer_forward(x, *past_of_layer(layer), *(p[layer] for p in weights))
        rows.append(r)
    new_rows = tuple(jnp.stack(list(col), axis=0) for col in zip(*rows))
    return x, new_rows

def setup_inputs(seed: int = 0) -> dict:
    key = jax.random.key(seed)
    ks = jax.random.split(key, 24)
    nrm = lambda k, shape, s=1.0: jax.random.normal(k, shape, jnp.float32) * s
    cache_len = N_META + PAST_LEN
    return {
        "x_prompt": nrm(ks[0], (BATCH, SEQ, D_MODEL)),
        "x_sample": nrm(ks[1], (DEC_BATCH, DEC_SEQ, D_MODEL)),
        "cache_fox_k": nrm(ks[2], (DEPTH, DEC_BATCH, cache_len, FOX_HEADS, HEAD_DIM)),
        "cache_fox_v": nrm(ks[3], (DEPTH, DEC_BATCH, cache_len, FOX_HEADS, HEAD_DIM)),
        "cache_fox_logf": jax.nn.log_sigmoid(2.0 + nrm(ks[4], (DEPTH, DEC_BATCH, cache_len, FOX_HEADS), 0.5)),
        "cache_sb_k": nrm(ks[5], (DEPTH, DEC_BATCH, cache_len, SB_HEADS, HEAD_DIM)),
        "cache_sb_v": nrm(ks[6], (DEPTH, DEC_BATCH, cache_len, SB_HEADS, HEAD_DIM)),
        "meta_tokens": nrm(ks[7], (N_META, D_MODEL)),
        "norm_mix": 1.0 + nrm(ks[8], (DEPTH, D_MODEL), 0.02),
        "w_in": nrm(ks[9], (DEPTH, D_MODEL, IN_WIDTH), D_MODEL ** -0.5),
        "b_forget": 2.0 + nrm(ks[10], (DEPTH, FOX_HEADS), 0.1),
        "fox_q_norm": 1.0 + nrm(ks[11], (DEPTH, HEAD_DIM), 0.02),
        "fox_k_norm": 1.0 + nrm(ks[12], (DEPTH, HEAD_DIM), 0.02),
        "w_o_fox": nrm(ks[13], (DEPTH, FOX_WIDTH, D_MODEL), FOX_WIDTH ** -0.5),
        "w_o_sb": nrm(ks[14], (DEPTH, SB_WIDTH, D_MODEL), SB_WIDTH ** -0.5),
        "w_out": nrm(ks[15], (DEPTH, D_MODEL, D_MODEL), D_MODEL ** -0.5),
        "norm_ffn": 1.0 + nrm(ks[16], (DEPTH, D_MODEL), 0.02),
        "w_peer_q": nrm(ks[17], (DEPTH, D_MODEL, PEER_HEADS * PEER_DK), D_MODEL ** -0.5),
        "peer_sub_keys_1": nrm(ks[18], (DEPTH, PEER_N_KEYS, PEER_HALF), PEER_HALF ** -0.5),
        "peer_sub_keys_2": nrm(ks[19], (DEPTH, PEER_N_KEYS, PEER_HALF), PEER_HALF ** -0.5),
        "expert_u": nrm(ks[20], (DEPTH, PEER_N_EXPERTS, D_MODEL), D_MODEL ** -0.5),
        "expert_v": nrm(ks[21], (DEPTH, PEER_N_EXPERTS, D_MODEL), PEER_HEADS ** -0.5),
    }

def reference(x_prompt, x_sample, cache_fox_k, cache_fox_v, cache_fox_logf, cache_sb_k, cache_sb_v,
              meta_tokens, norm_mix, w_in, b_forget, fox_q_norm, fox_k_norm, w_o_fox, w_o_sb, w_out,
              norm_ffn, w_peer_q, peer_sub_keys_1, peer_sub_keys_2, expert_u, expert_v):
    weights = (norm_mix, w_in, b_forget, fox_q_norm, fox_k_norm, w_o_fox, w_o_sb, w_out,
               norm_ffn, w_peer_q, peer_sub_keys_1, peer_sub_keys_2, expert_u, expert_v)

    bsz = x_prompt.shape[0]
    dt = x_prompt.dtype
    meta = jnp.broadcast_to(meta_tokens.astype(dt)[None], (bsz, N_META, D_MODEL))
    x_full = jnp.concatenate([meta, x_prompt], axis=1)
    empty_fox = jnp.zeros((bsz, 0, FOX_HEADS, HEAD_DIM), dt)
    empty_logf = jnp.zeros((bsz, 0, FOX_HEADS), jnp.float32)
    empty_sb = jnp.zeros((bsz, 0, SB_HEADS, HEAD_DIM), dt)
    prompt_past = lambda layer: (empty_fox, empty_fox, empty_logf, empty_sb, empty_sb)
    y_full, (fk_p, fv_p, fl_p, sk_p, sv_p) = run_stack(x_full, prompt_past, weights)
    y_prompt = y_full[:, N_META:]

    sample_past = lambda layer: (cache_fox_k[layer], cache_fox_v[layer], cache_fox_logf[layer],
                                 cache_sb_k[layer], cache_sb_v[layer])
    y_sample, (fk_s, fv_s, fl_s, sk_s, sv_s) = run_stack(x_sample, sample_past, weights)

    return (y_prompt, y_sample, fk_p, fv_p, fl_p, sk_p, sv_p, fk_s, fv_s, fl_s, sk_s, sv_s)


_drawn_inputs = setup_inputs


def setup_inputs(seed=0):
    import zlib

    import numpy as np

    out = dict(_drawn_inputs(seed))
    spreads = {}
    factors = {'cache_fox_logf': 74.27,
     'norm_mix': 2.693,
     'fox_q_norm': 5.33,
     'fox_k_norm': 3.129,
     'norm_ffn': 4.852}
    for name, (base, spread) in spreads.items():
        noise = np.random.default_rng([zlib.crc32(name.encode()), seed]).standard_normal(out[name].shape)
        drawn = base * np.exp(spread * noise) if base else spread * noise
        out[name] = __import__('jax').numpy.asarray(drawn.astype(out[name].dtype))
    for name, factor in factors.items():
        out[name] = (out[name] * factor).astype(out[name].dtype)
    return out
```

```python
from contextlib import ExitStack

import concourse.bass as bass
from concourse import mybir

F32 = mybir.dt.float32
F32R = mybir.dt.float32r
BF16 = mybir.dt.bfloat16
U32 = mybir.dt.uint32
ALU = mybir.AluOpType
ACT = mybir.ActivationFunctionType
AX = mybir.AxisListType

P = 128
D = 1024
KD = D // P
HEADS = 8
DH = 64
WID = HEADS * DH
META = 16
NP = META + 1024
NS = 32
PAST = META + 1024
KS = PAST + NS
T = NP + NS
TILES = -(-T // P)
LAST = T - (TILES - 1) * P
NPL = NP - (TILES - 1) * P
EPS = 1e-6
MASK = -1e30
BANK = 512
START = 1

NK = 128
TOPK = 16
TP = TILES * P
WT = 64
WTAIL = T % (2 * WT)
GB = 2
NG = NK // GB


def rows_of(t):
    return P if t < TILES - 1 else LAST


def row_parts(t, first=0):
    if t < TILES - 1:
        return [(0, max(first - t * P, 0), P - max(first - t * P, 0), max(t * P, first) - first)]
    return [(0, 0, NPL, t * P - first), (1, NPL, NS, 0)]


def store_rows(eng, dests, src, t, sem, first=0):
    parts = row_parts(t, first)
    for which, r0, n, at in parts:
        eng.dma_start(dests[which][at:at + n, :], src[r0:r0 + n, :]).then_inc(sem, 16)
    return 16 * len(parts)


class Chain:

    def __init__(self, eng, sem, base=0):
        self.eng, self.sem, self.base, self.n = eng, sem, base, 0

    def __call__(self, ins):
        self.n += 1
        ins.then_inc(self.sem, 1)
        self.eng.wait_ge(self.sem, self.base + self.n)


def project(nc, io, dram, keep, consts):
    v_fox, v_sb = keep["v_fox"], keep["v_sb"]
    cq, cq_s = keep["cq"], keep["cq_s"]
    ident = consts["ident"]
    CH = 10
    NST, NPS = 4, 4
    with ExitStack() as ctx:
        sb = lambda n, s, d=F32: ctx.enter_context(nc.sbuf_tensor(n, s, d))
        sem = lambda n: ctx.enter_context(nc.semaphore(n))
        xg = sb("xg", [P, KD, T])
        g_mix = sb("g_mix", [P, KD])
        gam = sb("gam", [P, 2, DH])
        bf = sb("bf", [P, HEADS])
        wff = sb("wff", [P, KD, HEADS])
        win = sb("win", [P, 2, KD, BANK])
        xr = sb("xr", [P, 2, D])
        ss = sb("ss", [P, TILES])
        rstd = sb("rstd", [P, TILES])
        stage = sb("stage", [P, NST, BANK])
        sq = sb("sq", [P, BANK])
        hs = sb("hs", [P, 3, HEADS])
        tst = sb("tst", [P, 2, BANK])
        ffz = sb("ffz", [P, TILES, HEADS])
        ffa = sb("ffa", [P, TILES, HEADS])
        logf = sb("logf", [P, TILES, HEADS])
        lt = sb("lt", [HEADS, T])
        ls = sb("ls", [HEADS, KS])
        ct = sb("ct", [HEADS, NP])
        cs = sb("cs", [HEADS, KS])
        ones8 = sb("ones8", [HEADS, KS])
        ps = [ctx.enter_context(nc.psum_tensor(f"ps{i}", [P, BANK], F32)) for i in range(NPS)]
        pt = [ctx.enter_context(nc.psum_tensor(f"pt{i}", [P, BANK], F32)) for i in range(2)]
        pf = ctx.enter_context(nc.psum_tensor("pf", [P, BANK], F32))
        pc = ctx.enter_context(nc.psum_tensor("pc", [P, BANK], F32))

        small_in = sem("small_in")
        x_in = [sem(f"x_in{i}") for i in range(2)]
        xt_in = sem("xt_in")
        w_in_sem = [sem(f"w_in{i}") for i in range(2)]
        rows_sq = sem("rows_sq")
        ms_ready = sem("ms_ready")
        rt_ready = sem("rt_ready")
        rstd_ready = sem("rstd_ready")
        xg_ready = sem("xg_ready")
        proj_ready = sem("proj_ready")
        staged = sem("staged")
        cleared = sem("cleared")
        hms = sem("hms")
        hrt = sem("hrt")
        normed = sem("normed")
        turned = sem("turned")
        turned_out = sem("turned_out")
        t_stored = [sem(f"t_stored{i}") for i in range(2)]
        s_stored = [sem(f"s_stored{i}") for i in range(NST)]
        v_stored = sem("v_stored")
        dve_step = sem("dve_step")
        ff_ready = sem("ff_ready")
        ff_out = sem("ff_out")
        ffz_ready = sem("ffz_ready")
        ffl = sem("ffl")
        logf_ready = sem("logf_ready")
        lt_ready = sem("lt_ready")
        lt_out = sem("lt_out")
        c_ready = sem("c_ready")
        cq_ready = sem("cq_ready")
        cq_out = sem("cq_out")
        c_stored = sem("c_stored")

        QK = (0, 1, 3, 4)
        tiles = [(c, t) for c in range(CH) for t in range(TILES)]
        turn_no = {x: n for n, x in enumerate([x for x in tiles if x[0] in QK])}
        norm_no = {x: n for n, x in enumerate([x for x in tiles if x[0] in (0, 1)])}
        stored_at, total = {}, [0] * NST
        for n, (c, t) in enumerate(tiles):
            if c in (1, 4):
                total[n % NST] += 16 * len(row_parts(t))
            if c >= 6:
                total[n % NST] += 16
            stored_at[n] = total[n % NST]
        scratch = {0: dram["q_fox"], 1: dram["k_fox"], 3: dram["q_sb"], 4: dram["k_sb"]}

        with nc.Block() as block:

            @block.sync
            def _(sp):
                sp.dma_start(g_mix[:], io["norm_mix"]).then_inc(small_in, 16)
                sp.dma_start(gam[:, 0, :], io["fox_q_norm"].partition_broadcast(P)).then_inc(small_in, 16)
                sp.dma_start(gam[:, 1, :], io["fox_k_norm"].partition_broadcast(P)).then_inc(small_in, 16)
                sp.dma_start(bf[:], io["b_forget"].partition_broadcast(P)).then_inc(small_in, 16)
                sp.dma_start(wff[:], io["w_ff"].rearrange("(k p) n -> p k n", p=P)).then_inc(small_in, 16)
                sp.dma_start(ls[:, 0:PAST], io["cache_logf_t"]).then_inc(small_in, 16)
                for k in range(KD):
                    sp.dma_start(xg[:, k, :], io["x_t"][k * P:(k + 1) * P, :]).then_inc(xt_in, 16)
                for c in range(2):
                    sp.dma_start(win[:, c % 2], io["w_main"][:, c * BANK:(c + 1) * BANK]
                                 .rearrange("(k p) n -> p k n", p=P)).then_inc(w_in_sem[c % 2], 16)
                for t in range(TILES):
                    if t >= 2:
                        sp.wait_ge(rows_sq, t - 1)
                    sp.dma_start(xr[0:rows_of(t), t % 2, :], io["x"][t * P:t * P + rows_of(t), :]).then_inc(x_in[t % 2], 16)
                for c in range(2, CH):
                    sp.wait_ge(proj_ready, (c - 1) * TILES)
                    sp.dma_start(win[:, c % 2], io["w_main"][:, c * BANK:(c + 1) * BANK]
                                 .rearrange("(k p) n -> p k n", p=P)).then_inc(w_in_sem[c % 2], 16)

            @block.tensor
            def _(pe):
                def forget():
                    pe.wait_ge(small_in, 96)
                    for t in range(TILES):
                        for k in range(KD):
                            mm = nc.tensor.matmul(pf[0:rows_of(t), t * HEADS:(t + 1) * HEADS],
                                                  xg[:, k, t * P:t * P + rows_of(t)], wff[:, k, :],
                                                  start=k == 0, stop=k == KD - 1)
                    mm.then_inc(ff_ready, 1)

                def turn(c, t):
                    n, r = turn_no[c, t], rows_of(t)
                    if c in (0, 1):
                        pe.wait_ge(normed, norm_no[c, t] + 1)
                    else:
                        pe.wait_ge(staged, tiles.index((c, t)) + 1)
                    if n >= 2:
                        pe.wait_ge(turned_out, n - 1)
                    slot = tiles.index((c, t)) % NST
                    for g in range(4):
                        mm = nc.tensor.transpose(pt[n % 2][:, g * P:g * P + r],
                                                 stage[0:r, slot, g * P:(g + 1) * P], ident[0:r, 0:r])
                    mm.then_inc(turned, 1)

                pe.wait_ge(xg_ready, KD)
                forget()
                for n, (c, t) in enumerate(tiles):
                    if t == 0:
                        pe.wait_ge(w_in_sem[c % 2], 16 * (c // 2 + 1))
                    if n >= NPS:
                        pe.wait_ge(staged, n - NPS + 1)
                    for k in range(KD):
                        mm = nc.tensor.matmul(ps[n % NPS][0:rows_of(t), :], xg[:, k, t * P:t * P + rows_of(t)],
                                              win[:, c % 2, k, :], start=k == 0, stop=k == KD - 1)
                    mm.then_inc(proj_ready, 1)
                    if n and tiles[n - 1] in turn_no:
                        turn(*tiles[n - 1])
                pe.wait_ge(logf_ready, 1)
                for b, (t0, t1) in enumerate(((0, 4), (4, 8), (8, 9))):
                    if b:
                        pe.wait_ge(lt_out, b)
                    for t in range(t0, t1):
                        mm = nc.tensor.transpose(pf[0:HEADS, (t - t0) * P:(t - t0) * P + rows_of(t)],
                                                 logf[0:rows_of(t), t, :], ident[0:rows_of(t), 0:rows_of(t)])
                    mm.then_inc(lt_ready, 1)
                pe.wait_ge(c_ready, 2)
                for t in range(TILES):
                    n = min(P, NP - t * P)
                    nc.tensor.transpose(pc[0:n, t * HEADS:(t + 1) * HEADS], ct[:, t * P:t * P + n],
                                        ident[0:HEADS, 0:HEADS])
                nc.tensor.transpose(pc[0:NS, TILES * HEADS:(TILES + 1) * HEADS], cs[:, PAST:KS],
                                    ident[0:HEADS, 0:HEADS]).then_inc(cq_ready, 1)

            @block.scalar
            def _(act):
                act.wait_ge(cleared, 1)
                for t in range(TILES):
                    act.wait_ge(x_in[t % 2], 16 * (t // 2 + 1))
                    row = xr[0:rows_of(t), t % 2, :]
                    nc.scalar.activation(row, row, ACT.Square,
                                         accum_out=ss[0:rows_of(t), t:t + 1]).then_inc(rows_sq, 1)
                act.wait_ge(ms_ready, 1)
                nc.scalar.activation(rstd[:], ss[:], ACT.Sqrt).then_inc(rt_ready, 1)

                def root(c, t):
                    act.wait_ge(hms, norm_no[c, t] + 1)
                    nc.scalar.activation(hs[0:rows_of(t), 1, :], hs[0:rows_of(t), 0, :], ACT.Sqrt).then_inc(hrt, 1)

                def turn_out(c, t):
                    n, r = turn_no[c, t], rows_of(t)
                    act.wait_ge(turned, n + 1)
                    if n >= 2:
                        act.wait_ge(t_stored[n % 2], 16 * (n // 2))
                    src = pt[n % 2][:].rearrange("p (g t) -> p g t", g=4)[:, :, 0:r]
                    dst = tst[:, n % 2, :].rearrange("p (g t) -> p g t", g=4)[:, :, 0:r]
                    nc.scalar.activation(dst, src, ACT.Copy, scale=DH ** -0.5 if c in (0, 3) else 1.0).then_inc(turned_out, 1)

                act.wait_ge(rstd_ready, 1)
                for n, (c, t) in enumerate(tiles):
                    r = rows_of(t)
                    act.wait_ge(proj_ready, n + 1)
                    if c in (2, 5):
                        dst = (v_fox if c == 2 else v_sb)[0:r, t, :]
                    else:
                        dst = stage[0:r, n % NST, :]
                        if n >= NST:
                            before = tiles[n - NST]
                            if before in turn_no:
                                act.wait_ge(turned, turn_no[before] + 1)
                            if stored_at[n - NST]:
                                act.wait_ge(s_stored[n % NST], stored_at[n - NST])
                    nc.scalar.activation(dst, ps[n % NPS][0:r, :], ACT.Sigmoid if c >= 6 else ACT.Copy,
                                         scale=rstd[0:r, t:t + 1]).then_inc(staged, 1)
                    if n and tiles[n - 1] in norm_no:
                        root(*tiles[n - 1])
                    if n >= 2 and tiles[n - 2] in turn_no:
                        turn_out(*tiles[n - 2])
                act.wait_ge(ffz_ready, 1)
                nc.scalar.activation(ffa[:], ffa[:], ACT.Exp, scale=-1.0).then_inc(ffl, 1)
                act.wait_ge(ffl, 1)
                nc.scalar.activation(ffa[:], ffa[:], ACT.Ln, bias=1.0).then_inc(ffl, 1)
                for b, (t0, t1) in enumerate(((0, 4), (4, 8), (8, 9))):
                    w = sum(rows_of(t) for t in range(t0, t1))
                    act.wait_ge(lt_ready, b + 1)
                    nc.scalar.activation(lt[:, t0 * P:t0 * P + w], pf[0:HEADS, 0:w], ACT.Copy).then_inc(lt_out, 1)

            @block.vector
            def _(dve):
                step = Chain(dve, dve_step)
                nc.vector.memset(ss[:], 1.0).then_inc(cleared, 1)
                nc.vector.memset(ffz[:], 0.0).then_inc(cleared, 1)
                dve.wait_ge(cleared, 2)
                dve.wait_ge(small_in, 96)
                dve.wait_ge(xt_in, 16 * KD)
                for k in range(KD):
                    nc.vector.tensor_scalar(xg[:, k, :], xg[:, k, :], g_mix[:, k:k + 1], None, ALU.mult).then_inc(xg_ready, 1)
                step(nc.vector.memset(ones8[:], 1.0))
                dve.wait_ge(rows_sq, TILES)
                nc.vector.tensor_scalar(ss[:], ss[:], 1.0 / D, EPS, ALU.mult, ALU.add).then_inc(ms_ready, 1)
                dve.wait_ge(rt_ready, 1)
                nc.vector.reciprocal(rstd[:], rstd[:]).then_inc(rstd_ready, 1)
                dve.wait_ge(rstd_ready, 1)

                dve.wait_ge(ff_ready, 1)
                for t in range(TILES):
                    r = rows_of(t)
                    nc.vector.scalar_tensor_tensor(out=ffz[0:r, t, :], in0=pf[0:r, t * HEADS:(t + 1) * HEADS],
                                                   scalar=rstd[0:r, t:t + 1], in1=bf[0:r, :],
                                                   op0=ALU.mult, op1=ALU.add).then_inc(ff_out, 1)
                dve.wait_ge(ff_out, TILES)
                step(nc.vector.tensor_scalar(ffa[:], ffz[:], -1.0, None, ALU.mult))
                nc.vector.tensor_tensor(ffa[:], ffa[:], ffz[:], ALU.max).then_inc(ffz_ready, 1)

                for n, (c, t) in enumerate(tiles):
                    if c > 1:
                        break
                    r = rows_of(t)
                    row = stage[0:r, n % NST, :]
                    by_head = row.rearrange("p (h d) -> p h d", h=HEADS)
                    dve.wait_ge(staged, n + 1)
                    step(nc.vector.tensor_tensor(sq[0:r, :], row, row, ALU.mult))
                    step(nc.vector.tensor_reduce(hs[0:r, 0, :], sq[0:r, :].rearrange("p (h d) -> p h d", h=HEADS),
                                                 AX.X, ALU.add))
                    nc.vector.tensor_scalar(hs[0:r, 0, :], hs[0:r, 0, :], 1.0 / DH, EPS, ALU.mult, ALU.add).then_inc(hms, 1)
                    dve.wait_ge(hrt, n + 1)
                    step(nc.vector.reciprocal(hs[0:r, 2, :], hs[0:r, 1, :]))
                    step(nc.vector.tensor_tensor(by_head, by_head,
                                                 hs[0:r, 2, :].unsqueeze(2).to_broadcast([r, HEADS, DH]), ALU.mult))
                    nc.vector.tensor_tensor(by_head, by_head,
                                            gam[0:r, c, :].unsqueeze(1).to_broadcast([r, HEADS, DH]),
                                            ALU.mult).then_inc(normed, 1)

                dve.wait_ge(ffl, 2)
                step(nc.vector.tensor_scalar(ffz[:], ffz[:], 0.0, None, ALU.min))
                nc.vector.tensor_tensor(logf[:], ffz[:], ffa[:], ALU.subtract).then_inc(logf_ready, 1)
                dve.wait_ge(lt_out, 3)
                nc.vector.tensor_tensor_scan(ct[:], ones8[:, 0:NP], lt[:, 0:NP], 0.0, ALU.mult, ALU.add).then_inc(c_ready, 1)
                step(nc.vector.tensor_copy(ls[:, PAST:KS], lt[:, NP:T]))
                nc.vector.tensor_tensor_scan(cs[:], ones8[:], ls[:], 0.0, ALU.mult, ALU.add).then_inc(c_ready, 1)
                dve.wait_ge(cq_ready, 1)
                for t in range(TILES):
                    n = min(P, NP - t * P)
                    nc.vector.tensor_copy(cq[0:n, t, :], pc[0:n, t * HEADS:(t + 1) * HEADS]).then_inc(cq_out, 1)
                nc.vector.tensor_copy(cq_s[:], pc[0:NS, TILES * HEADS:(TILES + 1) * HEADS]).then_inc(cq_out, 1)

            @block.gpsimd
            def _(pool):
                def store_turned(c, t):
                    n, r = turn_no[c, t], rows_of(t)
                    pool.wait_ge(turned_out, n + 1)
                    pool.dma_start(scratch[c][:, t * P:t * P + r].rearrange("(g p) t -> p g t", p=P),
                                   tst[:, n % 2, :].rearrange("p (g t) -> p g t", g=4)[:, :, 0:r]).then_inc(t_stored[n % 2], 16)

                vs = 0
                for n, (c, t) in enumerate(tiles):
                    r = rows_of(t)
                    if c == 1:
                        pool.wait_ge(normed, norm_no[c, t] + 1)
                        store_rows(pool, (io["fk_p"], io["fk_s"]), stage[:, n % NST, :], t, s_stored[n % NST])
                    elif c > 1:
                        pool.wait_ge(staged, n + 1)
                    if c == 4:
                        store_rows(pool, (io["sk_p"], io["sk_s"]), stage[:, n % NST, :], t, s_stored[n % NST])
                    if c == 2:
                        vs += store_rows(pool, (io["fv_p"], io["fv_s"]), v_fox[:, t, :], t, v_stored)
                    if c == 5:
                        vs += store_rows(pool, (io["sv_p"], io["sv_s"]), v_sb[:, t, :], t, v_stored)
                    if c >= 6:
                        pool.dma_start(dram["gates"][t * P:t * P + r, (c - 6) * BANK:(c - 5) * BANK],
                                       stage[0:r, n % NST, :]).then_inc(s_stored[n % NST], 16)
                    if n >= 2 and tiles[n - 2] in turn_no:
                        store_turned(*tiles[n - 2])
                pool.wait_ge(logf_ready, 1)
                for t in range(TILES):
                    vs += store_rows(pool, (io["logf_p"], io["logf_s"]), logf[:, t, :], t, v_stored)
                pool.wait_ge(c_ready, 2)
                pool.dma_start(dram["c_p"], ct[:]).then_inc(c_stored, 16)
                pool.dma_start(dram["c_s"], cs[:]).then_inc(c_stored, 16)
                pool.wait_ge(c_stored, 32)
                pool.wait_ge(v_stored, vs)
                for i in range(NST):
                    pool.wait_ge(s_stored[i], total[i])
                for i in range(2):
                    pool.wait_ge(t_stored[i], 16 * (len(turn_no) // 2))
                pool.wait_ge(cq_out, TILES + 1)


QT = TILES + 1
KINDS = 2


def query_tile(i):
    if i == QT - 1:
        return NS, NP, KS, TILES
    n = min(P, NP - i * P)
    return n, i * P, i * P + n, i + 1


def attend(nc, io, dram, keep, consts):
    cq, cq_s = keep["cq"], keep["cq_s"]
    values = (keep["v_fox"], keep["v_sb"])
    past_values = (keep["pv_fox"], keep["pv_sb"])
    out_rows = (keep["o_fox"], keep["o_sb"])
    ident, ident_b, masks = consts["ident"], consts["ident_b"], consts["masks"]
    units = [(i, kind) for i in range(QT) for kind in range(KINDS)]
    U = len(units)
    TG = BANK // P
    pairs = [(n, b, min(TG, query_tile(i)[3] - b)) for n, (i, _) in enumerate(units)
             for b in range(0, query_tile(i)[3], TG)]
    G = len(pairs)
    WIDE = 2 * BANK

    def score_start(i, k):
        return 0 if k == 0 else 3 * BANK - (query_tile(i)[2] > WIDE) * P
    assert G % 2 == 0
    with ExitStack() as ctx:
        sb = lambda n, s, d=F32: ctx.enter_context(nc.sbuf_tensor(n, s, d))
        sem = lambda n: ctx.enter_context(nc.semaphore(n))
        qt = [sb(f"qt{k}", [DH, NP + P]) for k in range(KINDS)]
        kt = [sb(f"kt{k}", [DH, NP]) for k in range(KINDS)]
        kts = [sb(f"kts{k}", [DH, KS]) for k in range(KINDS)]
        ckb = sb("ckb", [P, NP])
        cksb = sb("cksb", [NS, KS])
        prob = [[sb(f"prob{k}{j}", [P, TP]) for j in range(2)] for k in range(KINDS)]
        vh = [[sb(f"vh{k}{j}", [P, TILES, DH]) for j in range(2)] for k in range(KINDS)]
        low = sb("low", [P, KS])
        soft = sb("soft", [P, KS])
        ones = sb("ones", [P, KS])
        probt = sb("probt", [P, 2, TILES, P])
        stat = sb("stat", [P, 2, 4])
        ps = ctx.enter_context(nc.psum_tensor("pscores", [P, 5 * BANK], F32))
        pt = ctx.enter_context(nc.psum_tensor("ptr", [P, 2, TG, P], F32))
        po = ctx.enter_context(nc.psum_tensor("po", [P, BANK], F32))

        past_in = sem("past_in")
        cleared = sem("cleared_a")
        vh_ready = sem("vh_ready")
        ones_ready = sem("ones_ready")
        head_in = [sem(f"head_in{k}") for k in range(KINDS)]
        scored = sem("scored")
        minimum = sem("minimum")
        magnitude = sem("magnitude")
        exponent = sem("exponent")
        probs = sem("probs")
        turned = sem("turned_b")
        turned_out = sem("turned_b_out")
        summed = sem("summed")
        inverted = sem("inverted")
        summed_out = sem("summed_out")
        act_step = sem("act_step_b")
        dve_step = sem("dve_step_b")
        ACT_STEPS = 2 * QT
        DVE_STEPS = 3 * QT

        with nc.Block() as block:

            @block.sync
            def _(sp):
                for k, src in enumerate((io["cache_fox_v"], io["cache_sb_v"])):
                    full = TILES - 1
                    sp.dma_start(past_values[k][:, 0:full, :],
                                 src[0:full * P, :].rearrange("(t p) n -> p t n", p=P)).then_inc(past_in, 16)
                    sp.dma_start(past_values[k][0:PAST - full * P, full, :], src[full * P:PAST, :]).then_inc(past_in, 16)
                    sp.dma_start(past_values[k][NPL:LAST, full, :], values[k][NPL:LAST, full, :]).then_inc(past_in, 16)
                sp.wait_ge(cleared, 10)
                with sp.Fori(0, HEADS) as h:
                    for k in range(KINDS):
                        q, key, past = ((dram["q_fox"], dram["k_fox"], io["cache_fox_k_t"]),
                                        (dram["q_sb"], dram["k_sb"], io["cache_sb_k_t"]))[k]
                        sp.wait_ge(scored, h * U + START)
                        sp.dma_start(qt[k][:, 0:T], q[bass.ds(h * DH, DH), :]).then_inc(head_in[k], 16)
                        sp.dma_start(kt[k][:], key[bass.ds(h * DH, DH), 0:NP]).then_inc(head_in[k], 16)
                        sp.dma_start(kts[k][:, 0:PAST], past[bass.ds(h * DH, DH), :]).then_inc(head_in[k], 16)
                        sp.dma_start(kts[k][:, PAST:KS], key[bass.ds(h * DH, DH), NP:T]).then_inc(head_in[k], 16)
                        if k == 0:
                            sp.wait_ge(minimum, h * QT + START)
                            sp.dma_start(ckb[:], dram["c_p"][bass.ds(h, 1), :].to_broadcast([P, NP])).then_inc(head_in[k], 16)
                            sp.dma_start(cksb[:], dram["c_s"][bass.ds(h, 1), :].to_broadcast([NS, KS])).then_inc(head_in[k], 16)

            @block.tensor
            def _(pe):
                pe.sem_inc(summed, START)
                pe.sem_inc(scored, START)
                pe.wait_ge(cleared, 10)
                with pe.Fori(0, HEADS) as h:

                    def scores(n):
                        i, k = units[n]
                        r, q0, w, blocks = query_tile(i)
                        keys = kts[k] if i == QT - 1 else kt[k]
                        diag = w - r
                        if i == 0:
                            pe.wait_ge(head_in[k], (96, 64)[k] * (h + 1))
                        if k == 0 or w > WIDE:
                            pe.wait_ge(minimum, (h * QT + (i if k == 0 else i + 1)) + START)
                        if k == 1 or w > WIDE:
                            pe.wait_ge(exponent, h * QT + i + START)
                        s0 = score_start(i, k)
                        c0 = 0
                        while c0 < w:
                            c1 = min(w, c0 + BANK - (s0 + c0) % BANK)
                            masked = c1 > diag
                            mm = nc.tensor.matmul(ps[:, s0 + c0:s0 + c1], qt[k][:, q0:q0 + P], keys[:, c0:c1],
                                                  start=True, stop=not masked)
                            if masked:
                                m0 = max(diag, c0)
                                mm = nc.tensor.matmul(ps[:, s0 + m0:s0 + c1], ident_b[:],
                                                      masks[:, k, m0 - diag:c1 - diag], start=False, stop=True)
                            c0 = c1
                        mm.then_inc(scored, 1)

                    def turn(g):
                        n, b, count = pairs[g]
                        i, k = units[n]
                        r, _, w, blocks = query_tile(i)
                        if b == 0:
                            pe.wait_ge(probs, h * U + n + 1)
                        pe.wait_ge(turned_out, (h * G + g - 1 if g >= 2 else h * G) + START)
                        for j in range(count):
                            mm = nc.tensor.transpose(pt[:, g % 2, j, :], prob[k][i % 2][:, (b + j) * P:(b + j + 1) * P], ident[:])
                        mm.then_inc(turned, 1)

                    def weigh_values(g):
                        n, b, count = pairs[g]
                        i, k = units[n]
                        r, _, w, blocks = query_tile(i)
                        v = vh[k][i == QT - 1]
                        pe.wait_ge(turned_out, h * G + g + 1 + START)
                        if n == 0:
                            pe.wait_ge(vh_ready, 4 * (h + 1))
                        if b == 0:
                            pe.wait_ge(summed_out, h * U + n + START)
                        for j in range(count):
                            mm = nc.tensor.matmul(po[0:r, 0:DH], probt[:, n % 2, b + j, 0:r],
                                                  v[:, b + j, :], start=b + j == 0, stop=b + j == blocks - 1)
                        if b + count == blocks:
                            mm.then_inc(summed, 1)

                    scores(0)
                    scores(1)
                    scores(2)
                    done = 3
                    turn(0)
                    for g in range(G):
                        if g + 1 < G:
                            if pairs[g + 1][1] == 0 and done < U:
                                scores(done)
                                done += 1
                            turn(g + 1)
                        weigh_values(g)

            @block.scalar
            def _(act):
                act.sem_inc(summed_out, START)
                act.sem_inc(turned_out, START)
                with act.Fori(0, HEADS) as h:
                    step = Chain(act, act_step, h * ACT_STEPS)

                    def magnitudes(n):
                        i, k = units[n]
                        r, _, w, _ = query_tile(i)
                        if k == 0:
                            return
                        act.wait_ge(scored, h * U + n + 1 + START)
                        act.wait_ge(exponent, h * QT + i + START)
                        step(nc.scalar.activation(low[0:r, 0:w], ps[0:r, score_start(i, k):score_start(i, k) + w], ACT.Abs))
                        step(nc.scalar.activation(low[0:r, 0:w], low[0:r, 0:w], ACT.Exp, scale=-1.0))
                        nc.scalar.activation(low[0:r, 0:w], low[0:r, 0:w], ACT.Ln, bias=1.0).then_inc(magnitude, 1)

                    def probabilities(n):
                        i, k = units[n]
                        r, _, w, _ = query_tile(i)
                        p = prob[k][i % 2][0:r, 0:w]
                        if k == 0:
                            act.wait_ge(minimum, h * QT + i + 1 + START)
                            nc.scalar.activation(p, p, ACT.Exp, scale=-1.0, bias=stat[0:r, i % 2, 0:1],
                                                 accum_out=stat[0:r, i % 2, 1:2]).then_inc(probs, 1)
                        else:
                            act.wait_ge(exponent, h * QT + i + 1 + START)
                            nc.scalar.activation(p, p, ACT.Exp).then_inc(probs, 1)

                    def turn_out(n):
                        for g, (m, b, count) in enumerate(pairs):
                            if m != n:
                                continue
                            i, k = units[n]
                            r, _, w, blocks = query_tile(i)
                            act.wait_ge(turned, h * G + g + 1)
                            if b == 0:
                                act.wait_ge(summed, (h * U + n - 1 if n >= 2 else h * U) + START)
                            nc.scalar.activation(probt[:, n % 2, b:b + count, 0:r], pt[:, g % 2, 0:count, 0:r],
                                                 ACT.Copy).then_inc(turned_out, 1)

                    def take_output(n):
                        i, k = units[n]
                        r = query_tile(i)[0]
                        dst = out_rows[k][0:r, i, bass.ds(h * DH, DH)]
                        if k == 0:
                            act.wait_ge(inverted, h * QT + i + 1)
                        act.wait_ge(summed, h * U + n + 1 + START)
                        nc.scalar.activation(dst, po[0:r, 0:DH], ACT.Copy,
                                             scale=1.0 if k else stat[0:r, i % 2, 2:3]).then_inc(summed_out, 1)

                    magnitudes(1)
                    probabilities(0)
                    for n in range(1, U + 1):
                        if n + 1 < U:
                            magnitudes(n + 1)
                        if n < U:
                            probabilities(n)
                        if n >= 2:
                            take_output(n - 2)
                        turn_out(n - 1)
                    take_output(U - 1)
                    assert step.n == ACT_STEPS, step.n

            @block.gpsimd
            def _(pool):
                for k in range(KINDS):
                    nc.gpsimd.memset(qt[k][:, T:], 0.0).then_inc(cleared, 1)
                    for j in range(2):
                        nc.gpsimd.memset(prob[k][j][:], 0.0).then_inc(cleared, 1)
                        nc.gpsimd.memset(vh[k][j][:], 0.0).then_inc(cleared, 1)
                pool.wait_ge(cleared, 10)
                pool.wait_ge(past_in, 96)
                with pool.Fori(0, HEADS) as h:
                    pool.wait_ge(summed, h * U + START)
                    full = TILES - 1
                    for k in range(KINDS):
                        for j, v in enumerate((values[k], past_values[k])):
                            nc.gpsimd.tensor_copy(vh[k][j][:, 0:full, :], v[:, 0:full, bass.ds(h * DH, DH)])
                            nc.gpsimd.tensor_copy(vh[k][j][0:LAST, full, :],
                                                  v[0:LAST, full, bass.ds(h * DH, DH)]).then_inc(vh_ready, 1)

            @block.vector
            def _(dve):
                dve.sem_inc(exponent, START)
                dve.sem_inc(minimum, START)
                nc.vector.memset(ones[:], 1.0).then_inc(ones_ready, 1)
                dve.wait_ge(cleared, 10)
                dve.wait_ge(ones_ready, 1)
                with dve.Fori(0, HEADS) as h:
                    step = Chain(dve, dve_step, h * DVE_STEPS)

                    def invert(n):
                        i, r = units[n][0], query_tile(units[n][0])[0]
                        dve.wait_ge(probs, h * U + n + 1)
                        nc.vector.reciprocal(stat[0:r, i % 2, 2:3], stat[0:r, i % 2, 1:2]).then_inc(inverted, 1)

                    for n, (i, k) in enumerate(units):
                        r, _, w, _ = query_tile(i)
                        p = prob[k][i % 2][0:r, 0:w]
                        z = ps[0:r, score_start(i, k):score_start(i, k) + w]
                        if n >= 2 and k == 0:
                            invert(n - 2)
                        if n == 0 or n >= 4:
                            dve.wait_ge(summed, (h * U + n - 3 if n else h * U) + START)
                        if k == 0:
                            if i == 0:
                                dve.wait_ge(head_in[0], 96 * (h + 1))
                            dve.wait_ge(scored, h * U + n + 1 + START)
                            ck = (cksb if i == QT - 1 else ckb)[0:r, 0:w]
                            cqc = cq_s[0:r, bass.ds(h, 1)] if i == QT - 1 else cq[0:r, i, bass.ds(h, 1)]
                            step(nc.vector.scalar_tensor_tensor(out=p, in0=ck, scalar=cqc, in1=z,
                                                                op0=ALU.subtract, op1=ALU.subtract))
                            nc.vector.tensor_reduce(stat[0:r, i % 2, 0:1], p, AX.X, ALU.min).then_inc(minimum, 1)
                        else:
                            dve.wait_ge(magnitude, h * QT + i + 1)
                            step(nc.vector.scalar_tensor_tensor(out=soft[0:r, 0:w], in0=z, scalar=0.0,
                                                                in1=low[0:r, 0:w], op0=ALU.max, op1=ALU.add))
                            step(nc.vector.tensor_tensor_scan(p[:, ::-1], ones[0:r, 0:w], soft[0:r, 0:w][:, ::-1], 0.0,
                                                              ALU.mult, ALU.add))
                            nc.vector.tensor_tensor(p, z, p, ALU.subtract).then_inc(exponent, 1)
                    invert(U - 2)
                    assert step.n == DVE_STEPS, step.n


def merge(nc, io, dram, keep, consts):
    out_rows, acc, n2t = (keep["o_fox"], keep["o_sb"]), keep["acc"], keep["n2t"]
    ident = consts["ident"]
    with ExitStack() as ctx:
        sb = lambda n, s, d=F32: ctx.enter_context(nc.sbuf_tensor(n, s, d))
        sem = lambda n: ctx.enter_context(nc.semaphore(n))
        wo = [sb(f"wo{k}", [P, WID // P, D]) for k in range(KINDS)]
        wout = sb("wout", [P, KD, D])
        g_ffn = sb("g_ffn", [P, KD])
        gate = sb("gate", [P, KINDS, D])
        ot = sb("ot", [P, KINDS, WID // P, P])
        mt = sb("mt", [P, KD, P])
        hn = sb("hn", [P, D])
        st = sb("st", [P, 4])
        py = [ctx.enter_context(nc.psum_tensor(f"py{k}", [P, D], F32)) for k in range(KINDS)]
        ptt = ctx.enter_context(nc.psum_tensor("ptt", [P, KD, P], F32))
        ph = ctx.enter_context(nc.psum_tensor("ph", [P, D], F32))

        w_in = sem("w_in_m")
        g_in = sem("g_in")
        x_in = sem("x_in_m")
        gates_in = sem("gates_in")
        cleared = sem("cleared_m")
        o_turned, o_out = sem("o_turned"), sem("o_out")
        y_ready = sem("y_ready")
        merged = sem("merged")
        m_turned, m_out = sem("m_turned"), sem("m_out")
        h_ready = sem("h_ready")
        h_added = sem("h_added")
        h_sq = sem("h_sq")
        h_ms = sem("h_ms")
        h_rt = sem("h_rt")
        h_rs = sem("h_rs")
        h_normed = sem("h_normed")
        n_turned, n_out = sem("n_turned"), sem("n_out")
        step_m = sem("step_m")

        with nc.Block() as block:

            @block.sync
            def _(sp):
                for k, w in enumerate(("w_o_fox", "w_o_sb")):
                    sp.dma_start(wo[k][:], io[w].rearrange("(k p) n -> p k n", p=P)).then_inc(w_in, 16)
                sp.dma_start(wout[:], io["w_out"].rearrange("(k p) n -> p k n", p=P)).then_inc(w_in, 16)
                sp.dma_start(g_ffn[:], io["norm_ffn"]).then_inc(g_in, 16)
                sp.wait_ge(cleared, 2)
                full = TILES - 1
                sp.dma_start(acc[:, 0:full, :], io["x"][0:full * P, :].rearrange("(t p) n -> p t n", p=P)).then_inc(x_in, 16)
                sp.dma_start(acc[0:LAST, full, :], io["x"][full * P:T, :]).then_inc(x_in, 16)
                for t in range(TILES):
                    r = rows_of(t)
                    if t:
                        sp.wait_ge(m_turned, t)
                    sp.dma_start(gate[0:r], dram["gates"][t * P:t * P + r, :].rearrange("p (k n) -> p k n", k=KINDS)).then_inc(gates_in, 16)

            @block.tensor
            def _(pe):
                def turn_outputs(t):
                    if t:
                        pe.wait_ge(o_out, t)
                    if t >= 2:
                        pe.wait_ge(m_out, t - 1)
                    if t >= 3:
                        pe.wait_ge(n_out, t - 2)
                    for k in range(KINDS):
                        for g in range(4):
                            cols = slice(g * P, (g + 1) * P)
                            r = query_tile(t)[0]
                            mm = nc.tensor.transpose(ptt[:, k * 4 + g, 0:r],
                                                     out_rows[k][0:r, t, cols], ident[0:r, 0:r])
                            if t == TILES - 1:
                                mm = nc.tensor.transpose(ptt[:, k * 4 + g, r:r + NS],
                                                         out_rows[k][0:NS, QT - 1, cols],
                                                         ident[0:NS, 0:NS])
                    mm.then_inc(o_turned, 1)

                def project_outputs(t):
                    r = rows_of(t)
                    pe.wait_ge(o_out, t + 1)
                    if t:
                        pe.wait_ge(merged, t)
                    for k in range(KINDS):
                        for c in range(2):
                            for g in range(4):
                                mm = nc.tensor.matmul(py[k][0:r, c * BANK:(c + 1) * BANK], ot[:, k, g, 0:r],
                                                      wo[k][:, g, c * BANK:(c + 1) * BANK], start=g == 0, stop=g == 3)
                    mm.then_inc(y_ready, 1)

                def turn_merged(t):
                    r = rows_of(t)
                    pe.wait_ge(merged, t + 1)
                    pe.wait_ge(o_out, min(t + 2, TILES))
                    if t >= 2:
                        pe.wait_ge(n_out, t - 1)
                    for g in range(KD):
                        mm = nc.tensor.transpose(ptt[:, g, 0:r], gate[0:r, 0, g * P:(g + 1) * P], ident[0:r, 0:r])
                    mm.then_inc(m_turned, 1)

                def project_merged(t):
                    r = rows_of(t)
                    pe.wait_ge(m_out, t + 1)
                    if t:
                        pe.wait_ge(h_added, t)
                    for c in range(2):
                        for g in range(KD):
                            mm = nc.tensor.matmul(ph[0:r, c * BANK:(c + 1) * BANK], mt[:, g, 0:r],
                                                  wout[:, g, c * BANK:(c + 1) * BANK], start=g == 0, stop=g == KD - 1)
                    mm.then_inc(h_ready, 1)

                def turn_normed(t):
                    r = rows_of(t)
                    pe.wait_ge(h_normed, t + 1)
                    if t == TILES - 1:
                        pe.wait_ge(n_out, t)
                    pe.wait_ge(m_out, min(t + 2, TILES))
                    for g in range(KD):
                        mm = nc.tensor.transpose(ptt[:, g, 0:r], hn[0:r, g * P:(g + 1) * P], ident[0:r, 0:r])
                    mm.then_inc(n_turned, 1)

                pe.wait_ge(w_in, 48)
                for s in range(TILES + 2):
                    if s < TILES:
                        turn_outputs(s)
                        project_outputs(s)
                    if 1 <= s <= TILES:
                        turn_merged(s - 1)
                        project_merged(s - 1)
                    if s >= 2:
                        turn_normed(s - 2)

            @block.scalar
            def _(act):
                def norm_rows(t):
                    r = rows_of(t)
                    act.wait_ge(h_added, t + 1)
                    if t:
                        act.wait_ge(n_turned, t)
                    nc.scalar.activation(hn[0:r, :], acc[0:r, t, :], ACT.Square, accum_out=st[0:r, 0:1]).then_inc(h_sq, 1)
                    act.wait_ge(h_ms, t + 1)
                    nc.scalar.activation(st[0:r, 2:3], st[0:r, 1:2], ACT.Sqrt).then_inc(h_rt, 1)
                    act.wait_ge(h_rs, t + 1)
                    nc.scalar.activation(hn[0:r, :], acc[0:r, t, :], ACT.Copy, scale=st[0:r, 3:4]).then_inc(h_normed, 1)

                for s in range(TILES + 2):
                    if s < TILES:
                        r = rows_of(s)
                        act.wait_ge(o_turned, s + 1)
                        if s:
                            act.wait_ge(y_ready, s)
                        nc.scalar.activation(ot[:, :, :, 0:r], ptt[:, :, 0:r].rearrange("p (k g) t -> p k g t", k=KINDS),
                                             ACT.Copy).then_inc(o_out, 1)
                    if 1 <= s <= TILES:
                        r = rows_of(s - 1)
                        act.wait_ge(m_turned, s)
                        if s >= 2:
                            act.wait_ge(h_ready, s - 1)
                        nc.scalar.activation(mt[:, :, 0:r], ptt[:, :, 0:r], ACT.Copy).then_inc(m_out, 1)
                        norm_rows(s - 1)

            @block.vector
            def _(dve):
                step = Chain(dve, step_m)
                nc.vector.memset(acc[:, TILES - 1, :], 0.0).then_inc(cleared, 1)
                nc.vector.memset(n2t[:, :, T:TP], 0.0).then_inc(cleared, 1)
                dve.wait_ge(g_in, 16)
                dve.wait_ge(x_in, 32)
                for s in range(TILES + 2):
                    if s < TILES:
                        r = rows_of(s)
                        dve.wait_ge(gates_in, 16 * (s + 1))
                        dve.wait_ge(y_ready, s + 1)
                        for k in range(KINDS):
                            step(nc.vector.tensor_tensor(gate[0:r, k, :], gate[0:r, k, :], py[k][0:r, :], ALU.mult))
                        nc.vector.tensor_tensor(gate[0:r, 0, :], gate[0:r, 0, :], gate[0:r, 1, :], ALU.add).then_inc(merged, 1)
                    if 1 <= s <= TILES:
                        t = s - 1
                        r = rows_of(t)
                        dve.wait_ge(h_ready, t + 1)
                        nc.vector.tensor_tensor(acc[0:r, t, :], acc[0:r, t, :], ph[0:r, :], ALU.add).then_inc(h_added, 1)
                        dve.wait_ge(h_sq, t + 1)
                        nc.vector.tensor_scalar(st[0:r, 1:2], st[0:r, 0:1], 1.0 / D, EPS, ALU.mult, ALU.add).then_inc(h_ms, 1)
                        dve.wait_ge(h_rt, t + 1)
                        nc.vector.reciprocal(st[0:r, 3:4], st[0:r, 2:3]).then_inc(h_rs, 1)
                    if s >= 2:
                        t = s - 2
                        r = rows_of(t)
                        dve.wait_ge(n_turned, t + 1)
                        nc.vector.tensor_tensor(n2t[:, :, t * P:t * P + r], ptt[:, :, 0:r],
                                                g_ffn[:].unsqueeze(2).to_broadcast([P, KD, r]), ALU.mult).then_inc(n_out, 1)
                dve.wait_ge(n_out, TILES)


def retrieve(nc, io, dram, keep, consts):
    n2t = keep["n2t"]
    e_out, gw = (keep["e1"], keep["e2"]), keep["gw"]
    iota16 = consts["iota16"]
    QC = TP // 3
    with ExitStack() as ctx:
        sb = lambda n, s, d=F32: ctx.enter_context(nc.sbuf_tensor(n, s, d))
        sem = lambda n: ctx.enter_context(nc.semaphore(n))
        wq = [sb(f"wq{i}", [P, KD, P]) for i in range(2)]
        skt = sb("skt", [P, 2, NK])
        qh = [sb(f"qh{i}", [P, TP]) for i in range(2)]
        rest = sb("rest", [P, TILES, NK])
        top = sb("top", [P, 2, TILES, TOPK])
        idx = sb("idx", [P, 2, TILES, TOPK], U32)
        idf = sb("idf", [P, 2, TILES, TOPK])
        cand = sb("cand", [P, TILES, TOPK * TOPK])
        rest2 = sb("rest2", [P, TILES, TOPK * TOPK])
        sc = sb("sc", [P, TILES, TOPK])
        ci = sb("ci", [P, TILES, TOPK], U32)
        cab = sb("cab", [P, 2, TILES, TOPK], U32)
        caf = sb("caf", [P, 2, TILES, TOPK])
        hit = [sb(f"hit{i}", [P, TILES, TOPK, TOPK]) for i in range(2)]
        ex = sb("ex", [P, TILES, TOPK])
        sm = sb("sm", [P, 2, TILES])
        pq = [ctx.enter_context(nc.psum_tensor(f"pq{i}", [P, BANK], F32)) for i in range(2)]
        psc = [ctx.enter_context(nc.psum_tensor(f"psc{i}", [P, 3 * BANK], F32)) for i in range(2)]

        sk_in = sem("sk_in")
        wq_in = [sem(f"wq_in{i}") for i in range(2)]
        q_ready, q_out = sem("q_ready"), sem("q_out")
        s_ready = sem("s_ready")
        s_used = sem("s_used")
        picked = sem("picked")
        shifted = sem("shifted")
        expd = sem("expd")

        with nc.Block() as block:

            @block.sync
            def _(sp):
                for i, name in enumerate(("sub_keys_1_t", "sub_keys_2_t")):
                    sp.dma_start(skt[:, i, :], io[name]).then_inc(sk_in, 16)
                with sp.Fori(0, HEADS) as h:
                    for i in range(2):
                        sp.wait_ge(q_ready, h * 6 + START)
                        sp.dma_start(wq[i][:], io["w_peer_q"][:, bass.ds(h * 2 * P + i * P, P)]
                                     .rearrange("(k p) n -> p k n", p=P)).then_inc(wq_in[i], 16)

            @block.tensor
            def _(pe):
                pe.sem_inc(s_ready, START)
                pe.sem_inc(q_ready, START)
                pe.wait_ge(sk_in, 32)
                with pe.Fori(0, HEADS) as h:

                    def queries(i):
                        pe.wait_ge(wq_in[i], 16 * (h + 1))
                        for c in range(3):
                            n = i * 3 + c
                            pe.wait_ge(q_out, (h * 6 + n - 1 if n >= 2 else h * 6) + START)
                            for k in range(KD):
                                mm = nc.tensor.matmul(pq[n % 2][:, 0:QC], wq[i][:, k, :], n2t[:, k, c * QC:(c + 1) * QC],
                                                      start=k == 0, stop=k == KD - 1)
                            mm.then_inc(q_ready, 1)

                    def scores(i):
                        pe.wait_ge(q_out, h * 6 + 3 * i + 3 + START)
                        pe.wait_ge(s_used, h * 2 + i + START)
                        for t in range(TILES):
                            mm = nc.tensor.matmul(psc[i][:, t * NK:(t + 1) * NK], qh[i][:, t * P:(t + 1) * P],
                                                  skt[:, i, :], start=True, stop=True)
                        mm.then_inc(s_ready, 1)

                    queries(0)
                    queries(1)
                    scores(0)
                    scores(1)

            @block.scalar
            def _(act):
                act.sem_inc(q_out, START)
                with act.Fori(0, HEADS) as h:
                    for n in range(6):
                        act.wait_ge(q_ready, h * 6 + n + 1 + START)
                        if n % 3 == 0:
                            act.wait_ge(s_ready, h * 2 + START)
                        nc.scalar.activation(qh[n // 3][:, n % 3 * QC:(n % 3 + 1) * QC], pq[n % 2][:, 0:QC],
                                             ACT.Copy).then_inc(q_out, 1)
                    act.wait_ge(shifted, h + 1)
                    nc.scalar.activation(ex[:], ex[:], ACT.Exp).then_inc(expd, 1)

            @block.vector
            def _(dve):
                dve.sem_inc(s_used, START)
                with dve.Fori(0, HEADS) as h:
                    count = [0]

                    def mark(ins):
                        ins.then_inc(picked, 1)
                        count[0] += 1
                        return count[0]

                    def top16(values, scores, left, index):
                        first = [mark(nc.vector.max(values(t)[:, 0:8], scores(t))) for t in range(TILES)]
                        taken = []
                        for t in range(TILES):
                            dve.wait_ge(picked, first[t])
                            mark(nc.vector.max_index(index(t)[:, 0:8], values(t)[:, 0:8], scores(t)))
                            taken.append(mark(nc.vector.match_replace(left(t), values(t)[:, 0:8], scores(t), -3.0e38)))
                        second = []
                        for t in range(TILES):
                            dve.wait_ge(picked, taken[t])
                            second.append(mark(nc.vector.max(values(t)[:, 8:16], left(t))))
                        for t in range(TILES):
                            dve.wait_ge(picked, second[t])
                            last = mark(nc.vector.max_index(index(t)[:, 8:16], values(t)[:, 8:16], left(t)))
                        return last

                    for i in range(2):
                        dve.wait_ge(s_ready, h * 2 + i + 1 + START)
                        mark(nc.vector.memset(sm[:], 0.0))
                        last = top16(lambda t: top[:, i, t, :], lambda t: psc[i][:, t * NK:(t + 1) * NK],
                                     lambda t: rest[:, t, :], lambda t: idx[:, i, t, :])
                        dve.wait_ge(picked, last)
                        nc.vector.tensor_copy(idf[:, i], idx[:, i]).then_inc(s_used, 1)
                    grid = [P, TILES, TOPK, TOPK]
                    last = mark(nc.vector.tensor_tensor(cand[:].rearrange("p t (a b) -> p t a b", a=TOPK),
                                                        top[:, 0].unsqueeze(3).to_broadcast(grid),
                                                        top[:, 1].unsqueeze(2).to_broadcast(grid), ALU.add))
                    dve.wait_ge(picked, last)
                    last = top16(lambda t: sc[:, t, :], lambda t: cand[:, t, :],
                                 lambda t: rest2[:, t, :], lambda t: ci[:, t, :])
                    dve.wait_ge(picked, last)
                    nc.vector.tensor_tensor(ex[:], sc[:], sc[:, :, 0:1].to_broadcast([P, TILES, TOPK]),
                                            ALU.subtract).then_inc(shifted, 1)
                    mark(nc.vector.tensor_scalar(cab[:, 0], ci[:], 4, None, ALU.logical_shift_right))
                    last = mark(nc.vector.tensor_scalar(cab[:, 1], ci[:], TOPK - 1, None, ALU.bitwise_and))
                    dve.wait_ge(picked, last)
                    last = mark(nc.vector.tensor_copy(caf[:], cab[:]))
                    dve.wait_ge(picked, last)
                    dve.wait_ge(s_used, h * 2 + 2 + START)
                    for i in range(2):
                        last = mark(nc.vector.tensor_tensor(hit[i][:], caf[:, i].unsqueeze(3).to_broadcast(grid),
                                                            iota16[:].unsqueeze(1).unsqueeze(1).to_broadcast(grid), ALU.is_equal))
                    dve.wait_ge(picked, last)
                    for i in range(2):
                        last = mark(nc.vector.tensor_tensor(hit[i][:], hit[i][:], idf[:, i].unsqueeze(2).to_broadcast(grid), ALU.mult))
                    dve.wait_ge(picked, last)
                    for i in range(2):
                        mark(nc.vector.tensor_reduce(e_out[i][:, :, bass.ds(h, 1), :], hit[i][:], AX.X, ALU.add))
                    dve.wait_ge(expd, h + 1)
                    last = mark(nc.vector.tensor_reduce(sm[:, 0, :], ex[:], AX.X, ALU.add))
                    dve.wait_ge(picked, last)
                    last = mark(nc.vector.reciprocal(sm[:, 1, :], sm[:, 0, :]))
                    dve.wait_ge(picked, last)
                    mark(nc.vector.tensor_tensor(gw[:, :, bass.ds(h, 1), :], ex[:].unsqueeze(2),
                                                 sm[:, 1, :].unsqueeze(2).unsqueeze(3).to_broadcast([P, TILES, 1, TOPK]), ALU.mult))
                    dve.wait_ge(picked, count[0])
                    dve.sem_clear(picked)


def weigh(nc, io, dram, keep, consts):
    picks = (keep["e1"], keep["e2"], keep["gw"])
    ident, iota = consts["ident"], consts["iota"]
    BATCH = 8
    with ExitStack() as ctx:
        sb = lambda n, s, d=F32: ctx.enter_context(nc.sbuf_tensor(n, s, d))
        sem = lambda n: ctx.enter_context(nc.semaphore(n))
        pick_t = sb("pick_t", [P, 3, TP])
        hot1 = sb("hot1", [P, 2 * BATCH, NK])
        hot2 = sb("hot2", [P, 2 * BATCH, NK])
        table = [sb(f"table{i}", [P, NG, WT, GB]) for i in range(2)]
        pw = ctx.enter_context(nc.psum_tensor("pw", [P, 4, BATCH // 4 * BANK], F32))

        turned, turned_out = sem("turned_w"), sem("turned_w_out")
        hot = sem("hot")
        spread = sem("spread")
        taken = sem("taken")
        t_stored = [sem(f"table_stored{i}") for i in range(2)]
        PB = WT // BATCH
        TB = WTAIL // BATCH
        assert WTAIL % BATCH == 0 and WTAIL < WT
        LOTS = T // WT

        with nc.Block() as block:

            @block.tensor
            def _(pe):
                pe.sem_inc(spread, START)
                for j in range(3):
                    for t in range(TILES):
                        n = j * TILES + t
                        if n >= 4:
                            pe.wait_ge(turned_out, n - 3)
                        nc.tensor.transpose(pw[:, n % 4, 0:P], picks[j][:, t].rearrange("p h k -> p (h k)"),
                                            ident[:]).then_inc(turned, 1)

                def lot(first, batches):
                    for b in range(batches):
                        pe.wait_ge(hot, first + b + 1)
                        if b >= 4 or not isinstance(first, int) or first:
                            pe.wait_ge(taken, (first + b - 3 if b >= 4 or isinstance(first, int) else first) + START)
                        for j in range(BATCH):
                            s = b % 2 * BATCH + j
                            mm = nc.tensor.matmul(pw[:, b % 4, j * NK:(j + 1) * NK], hot2[:, s, :], hot1[:, s, :],
                                                  start=True, stop=True)
                        mm.then_inc(spread, 1)

                pe.wait_ge(turned_out, 3 * TILES)
                with pe.Fori(0, LOTS // 2) as i:
                    for half in range(2):
                        lot((2 * i + half) * PB, PB)
                lot(LOTS * PB, TB)

            @block.vector
            def _(dve):
                dve.wait_ge(turned_out, 3 * TILES)

                def lot(first, token, batches):
                    for b in range(batches):
                        if b >= 2 or not isinstance(first, int) or first:
                            dve.wait_ge(spread, (first + b - 1 if b >= 2 or isinstance(first, int) else first) + START)
                        for j in range(BATCH):
                            s = b % 2 * BATCH + j
                            at = bass.ds(token + b * BATCH + j, 1)
                            nc.vector.tensor_scalar(hot1[:, s, :], iota[:], pick_t[:, 0, at], pick_t[:, 2, at],
                                                    ALU.is_equal, ALU.mult)
                            ins = nc.vector.tensor_scalar(hot2[:, s, :], iota[:], pick_t[:, 1, at], None, ALU.is_equal)
                        ins.then_inc(hot, 1)

                with dve.Fori(0, LOTS // 2) as i:
                    for half in range(2):
                        lot((2 * i + half) * PB, (2 * i + half) * WT, PB)
                lot(LOTS * PB, LOTS * WT, TB)

            @block.scalar
            def _(act):
                act.sem_inc(taken, START)
                for j in range(3):
                    for t in range(TILES):
                        n = j * TILES + t
                        act.wait_ge(turned, n + 1)
                        nc.scalar.activation(pick_t[:, j, t * P:(t + 1) * P], pw[:, n % 4, 0:P], ACT.Copy).then_inc(turned_out, 1)

                def lot(first, half, batches, stored):
                    for b in range(batches):
                        if b == 0:
                            act.wait_ge(t_stored[half], stored + START)
                        act.wait_ge(spread, first + b + 1 + START)
                        nc.scalar.activation(table[half][:, :, b * BATCH:(b + 1) * BATCH, :].rearrange("p g t b -> p t g b"),
                                             pw[:, b % 4, :].rearrange("p (t g b) -> p t g b", t=BATCH, b=GB),
                                             ACT.Copy).then_inc(taken, 1)

                with act.Fori(0, LOTS // 2) as i:
                    for half in range(2):
                        lot((2 * i + half) * PB, half, PB, 16 * i)
                lot(LOTS * PB, 0, TB, 16 * (LOTS // 2))

            @block.sync
            def _(sp):
                for half in range(2):
                    sp.sem_inc(t_stored[half], START)

                def store(first, token, half, tokens):
                    sp.wait_ge(taken, first + tokens // BATCH + START)
                    sp.dma_start(dram["table"].rearrange("g p (t b) -> p g t b", b=GB)[:, :, bass.ds(token, tokens), :],
                                 table[half][:, :, 0:tokens, :]).then_inc(t_stored[half], 16)

                with sp.Fori(0, LOTS // 2) as i:
                    for half in range(2):
                        store((2 * i + half) * PB, (2 * i + half) * WT, half, WT)
                store(LOTS * PB, LOTS * WT, 0, WTAIL)
                sp.wait_ge(t_stored[0], 16 * (LOTS // 2 + 1) + START)
                sp.wait_ge(t_stored[1], 16 * (LOTS // 2) + START)


def split_tokens(nc, keep):
    with ExitStack() as ctx:
        high = ctx.enter_context(nc.semaphore("n2_high"))
        low = ctx.enter_context(nc.semaphore("n2_low"))
        with nc.Block() as block:

            @block.scalar
            def _(act):
                for k in range(KD):
                    nc.scalar.activation(keep["n2h"][:, k, :], keep["n2t"][:, k, 0:T], ACT.Copy).then_inc(high, 1)

            @block.vector
            def _(dve):
                for k in range(KD):
                    dve.wait_ge(high, k + 1)
                    nc.vector.tensor_tensor(keep["n2l"][:, k, :], keep["n2t"][:, k, 0:T],
                                            keep["n2h"][:, k, :].bitcast(F32), ALU.subtract).then_inc(low, 1)
                dve.wait_ge(low, KD)


def experts(nc, io, dram, keep, consts):
    acc, n2 = keep["acc"], (keep["n2h"], keep["n2l"])
    CC = 3
    CW = -(-T // CC // 2) * 2
    chunks = [(c * CW, min((c + 1) * CW, T)) for c in range(CC)]
    AR = GB * CC
    NA = 3
    GE = GB * NK
    PARTS = ((0, 0), (0, 1), (1, 0))
    assert AR % NA == 0 and NG % 2 == 0
    with ExitStack() as ctx:
        sb = lambda n, s, d=F32: ctx.enter_context(nc.sbuf_tensor(n, s, d))
        sem = lambda n: ctx.enter_context(nc.semaphore(n))
        u_raw = sb("u_raw", [P, KD, GE])
        v_raw = sb("v_raw", [P, GB, D])
        u = [sb(f"u_part{i}", [P, KD, GE], F32R) for i in range(2)]
        v = [sb(f"v_part{i}", [P, GB, D], F32R) for i in range(2)]
        wt = sb("wt", [P, T, GB])
        hh = [[sb(f"hh{s}{i}", [P, GB, TP], F32R) for i in range(2)] for s in range(2)]
        ge = sb("ge", [P, NA, CW])
        pa = [ctx.enter_context(nc.psum_tensor(f"pa{i}", [P, BANK], F32)) for i in range(NA)]
        py = [ctx.enter_context(nc.psum_tensor(f"pv{i}", [P, D], F32)) for i in range(2)]

        u_in, v_in, t_in = sem("u_in"), sem("v_in"), sem("t_in")
        u_high, u_split = sem("u_high"), sem("u_split")
        v_high, v_split = sem("v_high"), sem("v_split")
        product = sem("product")
        gelu = sem("gelu")
        weighted = sem("weighted")
        h_high, h_split = sem("h_high"), sem("h_split")
        valued = sem("valued")
        added = sem("added")
        padded = sem("padded")
        out_stored = sem("out_stored")

        with nc.Block() as block:

            @block.sync
            def _(sp):
                def load(g, first=False):
                    if not first:
                        sp.wait_ge(u_split, g)
                    sp.dma_start(u_raw[:], io["expert_u_t"][:, bass.ds(g * GE, GE)].rearrange("(k p) e -> p k e", p=P)).then_inc(u_in, 16)
                    if not first:
                        sp.wait_ge(weighted, g * AR)
                    sp.dma_start(wt[:], dram["table"][bass.ds(g, 1)].rearrange("g p (t b) -> p (g t) b", b=GB)).then_inc(t_in, 16)
                    if not first:
                        sp.wait_ge(v_split, g)
                    sp.dma_start(v_raw[:], io["expert_v"][bass.ds(g * GE, GE), :].rearrange("(b p) n -> p b n", p=P)).then_inc(v_in, 16)

                load(0, first=True)
                with sp.Fori(1, NG) as g:
                    load(g)
                for t in range(TILES):
                    sp.wait_ge(added, (NG - 1) * TILES + t + 1 + START)
                    for which, r0, n, at in row_parts(t, META):
                        sp.dma_start((io["y_p"], io["y_s"])[which][at:at + n, :], acc[r0:r0 + n, t, :]).then_inc(out_stored, 16)
                sp.wait_ge(out_stored, 16 * (TILES + 1))

            @block.tensor
            def _(pe):
                def activations(g, first=False):
                    pe.wait_ge(u_split, g + 1)
                    for b in range(GB):
                        for c, (c0, c1) in enumerate(chunks):
                            n = b * CC + c
                            if n >= NA or not first:
                                pe.wait_ge(gelu, g * AR + n - NA + 1)
                            for k in range(KD):
                                for j, (x, y) in enumerate(PARTS):
                                    mm = nc.tensor.matmul(pa[n % NA][:, 0:c1 - c0], u[x][:, k, b * P:(b + 1) * P],
                                                          n2[y][:, k, c0:c1], start=k == 0 and j == 0,
                                                          stop=k == KD - 1 and j == len(PARTS) - 1)
                            mm.then_inc(product, 1)

                def values(g, s):
                    pe.wait_ge(v_split, g + 1)
                    pe.wait_ge(h_split, (g + 1) * AR)
                    for t in range(TILES):
                        n = s * TILES + t
                        pe.wait_ge(added, (g * TILES + t - 1 if s == 1 or t >= 2 else g * TILES) + START)
                        for c in range(2):
                            for b in range(GB):
                                for j, (x, y) in enumerate(PARTS):
                                    mm = nc.tensor.matmul(py[n % 2][:, c * BANK:(c + 1) * BANK], hh[s][x][:, b, t * P:(t + 1) * P],
                                                          v[y][:, b, c * BANK:(c + 1) * BANK], start=b == 0 and j == 0,
                                                          stop=b == GB - 1 and j == len(PARTS) - 1)
                        mm.then_inc(valued, 1)

                pe.wait_ge(padded, 4)
                activations(0, first=True)
                with pe.Fori(0, NG // 2 - 1) as i:
                    for s in range(2):
                        activations(2 * i + s + 1)
                        values(2 * i + s, s)
                activations(NG - 1)
                values(NG - 2, 0)
                values(NG - 1, 1)

            @block.scalar
            def _(act):
                def split_u(g, first=False):
                    act.wait_ge(u_in, 16 * (g + 1))
                    if not first:
                        act.wait_ge(product, g * AR)
                    nc.scalar.activation(u[0][:], u_raw[:], ACT.Copy).then_inc(u_high, 1)

                def split_v(g, first=False):
                    act.wait_ge(v_in, 16 * (g + 1))
                    if not first:
                        act.wait_ge(valued, g * TILES)
                    nc.scalar.activation(v[0][:], v_raw[:], ACT.Copy).then_inc(v_high, 1)

                def group(g, s, early=0):
                    def high(n):
                        b, (c0, c1) = n // CC, chunks[n % CC]
                        act.wait_ge(weighted, g * AR + n + 1)
                        if n == 0 and early is None:
                            act.wait_ge(valued, (g - 1) * TILES)
                        nc.scalar.activation(hh[s][0][:, b, c0:c1], ge[:, n % NA, 0:c1 - c0], ACT.Copy).then_inc(h_high, 1)

                    for n in range(AR):
                        c0, c1 = chunks[n % CC]
                        act.wait_ge(product, g * AR + n + 1)
                        if n >= NA or early != 0:
                            act.wait_ge(h_split, g * AR + n - NA + 1)
                        nc.scalar.activation(ge[:, n % NA, 0:c1 - c0], pa[n % NA][:, 0:c1 - c0], ACT.Gelu).then_inc(gelu, 1)
                        if n:
                            high(n - 1)
                    high(AR - 1)

                split_u(0, first=True)
                group(0, 0, early=0)
                split_u(1)
                split_v(0, first=True)
                group(1, 1, early=1)
                split_u(2)
                split_v(1)
                with act.Fori(1, NG // 2 - 1) as i:
                    group(2 * i, 0, early=None)
                    split_u(2 * i + 1)
                    split_v(2 * i)
                    group(2 * i + 1, 1, early=None)
                    split_u(2 * i + 2)
                    split_v(2 * i + 1)
                group(NG - 2, 0, early=None)
                split_u(NG - 1)
                split_v(NG - 2)
                group(NG - 1, 1, early=None)
                split_v(NG - 1)

            @block.vector
            def _(dve):
                def rest_u(g):
                    dve.wait_ge(u_high, g + 1)
                    nc.vector.tensor_tensor(u[1][:], u_raw[:], u[0][:].bitcast(F32), ALU.subtract).then_inc(u_split, 1)

                def rest_v(g):
                    dve.wait_ge(v_high, g + 1)
                    nc.vector.tensor_tensor(v[1][:], v_raw[:], v[0][:].bitcast(F32), ALU.subtract).then_inc(v_split, 1)

                def weight(g, s):
                    def low(n):
                        b, (c0, c1) = n // CC, chunks[n % CC]
                        dve.wait_ge(h_high, g * AR + n + 1)
                        nc.vector.tensor_tensor(hh[s][1][:, b, c0:c1], ge[:, n % NA, 0:c1 - c0],
                                                hh[s][0][:, b, c0:c1].bitcast(F32), ALU.subtract).then_inc(h_split, 1)

                    dve.wait_ge(t_in, 16 * (g + 1))
                    for n in range(AR):
                        b, (c0, c1) = n // CC, chunks[n % CC]
                        dve.wait_ge(gelu, g * AR + n + 1)
                        x = ge[:, n % NA, 0:c1 - c0]
                        nc.vector.tensor_tensor(x, x, wt[:, c0:c1, b], ALU.mult).then_inc(weighted, 1)
                        if n:
                            low(n - 1)
                    low(AR - 1)

                def add(g, s):
                    for t in range(TILES):
                        r = rows_of(t)
                        dve.wait_ge(valued, g * TILES + t + 1)
                        nc.vector.tensor_tensor(acc[0:r, t, :], acc[0:r, t, :], py[(s * TILES + t) % 2][0:r, :],
                                                ALU.add).then_inc(added, 1)

                dve.sem_inc(added, START)
                for s in range(2):
                    for x in range(2):
                        nc.vector.memset(hh[s][x][:, :, T:TP].bitcast(F32), 0.0).then_inc(padded, 1)
                rest_u(0)
                weight(0, 0)
                rest_u(1)
                rest_v(0)
                with dve.Fori(0, NG // 2 - 1) as i:
                    for s in range(2):
                        weight(2 * i + s + 1, 1 - s)
                        rest_u(2 * i + s + 2)
                        add(2 * i + s, s)
                        rest_v(2 * i + s + 1)
                weight(NG - 1, 1)
                add(NG - 2, 0)
                rest_v(NG - 1)
                add(NG - 1, 1)


def constants(nc, consts):
    with ExitStack() as ctx:
        made = ctx.enter_context(nc.semaphore("made"))
        with nc.Block() as block:

            @block.gpsimd
            def _(pool):
                step = Chain(pool, made)
                ident, ident_b, masks = consts["ident"], consts["ident_b"], consts["masks"]
                step(nc.gpsimd.memset(ident[:], 0.0))
                step(nc.gpsimd.affine_select(out=ident[:], in_=ident[:], compare_op=ALU.not_equal, fill=1.0,
                                             base=0, pattern=[[-1, P]], channel_multiplier=1))
                step(nc.gpsimd.tensor_copy(ident_b[:], ident[:]))
                step(nc.gpsimd.memset(masks[:], 0.0))
                for k in range(KINDS):
                    step(nc.gpsimd.affine_select(out=masks[:, k], in_=masks[:, k], compare_op=ALU.is_ge, fill=MASK,
                                                 base=-k, pattern=[[-1, P]], channel_multiplier=1))
                step(nc.gpsimd.iota(consts["iota"][:], pattern=[[1, NK]], base=0, channel_multiplier=0,
                                    allow_small_or_imprecise_dtypes=True))
                step(nc.gpsimd.iota(consts["iota16"][:], pattern=[[1, TOPK]], base=0, channel_multiplier=0,
                                    allow_small_or_imprecise_dtypes=True))


def build(nc, io, upto=6):
    dram = {
        "q_fox": (WID, T), "k_fox": (WID, T), "q_sb": (WID, T), "k_sb": (WID, T),
        "gates": (T, KINDS * D), "c_p": (HEADS, NP), "c_s": (HEADS, KS), "table": (NG, NK, T * GB),
    }
    dram = {n: nc.dram_tensor(f"scratch_{n}", list(s), F32, kind="Internal").ap() for n, s in dram.items()}
    consts, keep = {}, {}
    with ExitStack() as ctx:
        def sb(c, group, n, s, d=F32, side="left"):
            group[n] = c.enter_context(nc.sbuf_tensor(n, s, d, side=side))

        sb(ctx, consts, "ident", [P, P])
        sb(ctx, consts, "ident_b", [P, P], BF16)
        sb(ctx, consts, "masks", [P, KINDS, P], BF16)
        sb(ctx, consts, "iota", [P, NK])
        sb(ctx, consts, "iota16", [P, TOPK])
        constants(nc, consts)
        with ExitStack() as outputs:
            with ExitStack() as inner:
                for n in ("o_fox", "o_sb"):
                    sb(outputs, keep, n, [P, QT, WID])
                for n in ("v_fox", "v_sb"):
                    sb(inner, keep, n, [P, TILES, WID])
                sb(inner, keep, "cq", [P, TILES, HEADS])
                sb(inner, keep, "cq_s", [NS, HEADS])
                project(nc, io, dram, keep, consts)
                for n in ("pv_fox", "pv_sb"):
                    sb(inner, keep, n, [P, TILES, WID])
                attend(nc, io, dram, keep, consts)
            sb(ctx, keep, "acc", [P, TILES, D], side="right")
            tokens = ExitStack()
            sb(tokens, keep, "n2t", [P, KD, TP], side="right")
            merge(nc, io, dram, keep, consts)
        with ExitStack() as picks:
            for n in ("e1", "e2", "gw"):
                sb(picks, keep, n, [P, TILES, HEADS, TOPK])
            retrieve(nc, io, dram, keep, consts)
            weigh(nc, io, dram, keep, consts)
        for n in ("n2h", "n2l"):
            sb(ctx, keep, n, [P, KD, T], F32R)
        split_tokens(nc, keep)
        tokens.close()
        experts(nc, io, dram, keep, consts)


OUTPUTS = [
    ("y_p", (NP - META, D), (1, NP - META, D)), ("y_s", (NS, D), (1, NS, D)),
    ("fk_p", (NP, WID), (1, 1, NP, HEADS, DH)), ("fv_p", (NP, WID), (1, 1, NP, HEADS, DH)),
    ("logf_p", (NP, HEADS), (1, 1, NP, HEADS)),
    ("sk_p", (NP, WID), (1, 1, NP, HEADS, DH)), ("sv_p", (NP, WID), (1, 1, NP, HEADS, DH)),
    ("fk_s", (NS, WID), (1, 1, NS, HEADS, DH)), ("fv_s", (NS, WID), (1, 1, NS, HEADS, DH)),
    ("logf_s", (NS, HEADS), (1, 1, NS, HEADS)),
    ("sk_s", (NS, WID), (1, 1, NS, HEADS, DH)), ("sv_s", (NS, WID), (1, 1, NS, HEADS, DH)),
]


def kernel(**inputs):
    import numpy as np
    import concourse.bacc as bacc
    from concourse.bass_utils import run_bass_kernel_spmd

    a = {n: np.asarray(x) for n, x in inputs.items()}
    x = np.concatenate([a["meta_tokens"], a["x_prompt"][0], a["x_sample"][0]], axis=0)
    w_in = a["w_in"][0]
    ff = 3 * WID
    turn = lambda m: m.transpose(1, 0)
    arrays = {
        "x": x, "x_t": turn(x),
        "w_main": np.concatenate([w_in[:, :ff], w_in[:, ff + HEADS:]], axis=1), "w_ff": w_in[:, ff:ff + HEADS],
        "norm_mix": turn(a["norm_mix"][0].reshape(KD, P)), "norm_ffn": turn(a["norm_ffn"][0].reshape(KD, P)), "b_forget": a["b_forget"][0],
        "fox_q_norm": a["fox_q_norm"][0], "fox_k_norm": a["fox_k_norm"][0],
        "cache_fox_k_t": turn(a["cache_fox_k"].reshape(PAST, WID)), "cache_fox_v": a["cache_fox_v"].reshape(PAST, WID),
        "cache_sb_k_t": turn(a["cache_sb_k"].reshape(PAST, WID)), "cache_sb_v": a["cache_sb_v"].reshape(PAST, WID),
        "cache_logf_t": turn(a["cache_fox_logf"].reshape(PAST, HEADS)),
        "w_o_fox": a["w_o_fox"][0], "w_o_sb": a["w_o_sb"][0], "w_out": a["w_out"][0], "w_peer_q": a["w_peer_q"][0],
        "sub_keys_1_t": turn(a["peer_sub_keys_1"][0]), "sub_keys_2_t": turn(a["peer_sub_keys_2"][0]),
        "expert_u_t": turn(a["expert_u"][0]), "expert_v": a["expert_v"][0],
    }
    arrays = {n: np.ascontiguousarray(v) for n, v in arrays.items()}
    nc = bacc.Bacc("TRN2", target_bir_lowering=False, num_devices=1)
    io = {n: nc.dram_tensor(n, list(v.shape), mybir.dt.from_np(v.dtype), kind="ExternalInput").ap() for n, v in arrays.items()}
    for n, shape, _ in OUTPUTS:
        io[n] = nc.dram_tensor(f"out_{n}", list(shape), F32, kind="ExternalOutput").ap()
    build(nc, io)
    r = run_bass_kernel_spmd(nc, [arrays], core_ids=[0])
    return tuple(r.results[0][f"out_{n}"].reshape(back) for n, _, back in OUTPUTS)
```
